# Optimizing a Trainium2 kernel written in Bass

```python
import math
import jax, jax.numpy as jnp
from jax import lax
import numpy as np

D_MODEL = 1024
BATCH = 1
SEQ = 1024
DEPTH = 2
DEC_BATCH = 8
DEC_SEQ = 1
PAST_LEN = 8192
PAGE_SIZE = 128

N_MIXERS = 2
N_DN_LAYERS = (DEPTH + 1) // 2
N_S5_LAYERS = DEPTH // 2

DN_QK_HEADS = 8
DN_V_HEADS = 16
DN_HEAD_K = 128
DN_HEAD_V = 128
DN_KEY_DIM = DN_QK_HEADS * DN_HEAD_K
DN_VAL_DIM = DN_V_HEADS * DN_HEAD_V
DN_CONV_DIM = 2 * DN_KEY_DIM + DN_VAL_DIM
DN_CONV_W = 4
DN_CHUNK = 64
DN_IN_DIM = DN_CONV_DIM + DN_VAL_DIM + 2 * DN_V_HEADS

S5_GROUP = 16
S5_GROUPS = D_MODEL // S5_GROUP
S5_STATE = 64

FFN_HIDDEN = -(-(8 * D_MODEL) // (3 * 256)) * 256
EPS = 1e-6

kernel_name = 'hybrid_gdn_s5_decoder_step'

def rmsnorm(x, g):
    xf = x.astype(jnp.float32)
    y = xf * lax.rsqrt(jnp.mean(xf * xf, axis=-1, keepdims=True) + EPS) * g.astype(jnp.float32)
    return y.astype(x.dtype)

def l2norm(x):
    return x * lax.rsqrt(jnp.sum(x * x, axis=-1, keepdims=True) + EPS)

def short_conv(x, buf, w):
    L = x.shape[1]
    xp = jnp.concatenate([buf, x], axis=1)
    y = xp[:, 0:L] * w[0]
    for j in range(1, DN_CONV_W):
        y = y + xp[:, j:j + L] * w[j]
    return jax.nn.silu(y), xp[:, L:]

def gated_delta_chunked(q, k, v, beta, g, s0):
    bsz, L, H, dk = q.shape
    dv = v.shape[-1]
    C = DN_CHUNK
    n = L // C

    def to_chunks(t):
        t = t.reshape((bsz, n, C) + t.shape[2:])
        return jnp.moveaxis(t, (1, 2), (0, 3))

    qc, kc, vc, bc, gc = map(to_chunks, (q, k, v, beta, g))
    gc = jnp.cumsum(gc, axis=-1)
    incl = jnp.tril(jnp.ones((C, C), dtype=bool))
    strict = jnp.tril(jnp.ones((C, C), dtype=bool), k=-1)
    diff = gc[..., :, None] - gc[..., None, :]
    decay = jnp.exp(jnp.where(incl, diff, -jnp.inf))
    kb = kc * bc[..., None]
    lmat = jnp.where(strict, jnp.einsum('nbhid,nbhjd->nbhij', kb, kc) * decay, 0.0)
    eye = jnp.eye(C, dtype=q.dtype)
    rhs = jnp.concatenate([kb * jnp.exp(gc)[..., None], vc * bc[..., None]], axis=-1)
    sol = lax.linalg.triangular_solve(eye + lmat, rhs, left_side=True, lower=True, unit_diagonal=True)
    wc, uc = sol[..., :dk], sol[..., dk:]
    qk = jnp.einsum('nbhid,nbhjd->nbhij', qc, kc) * decay

    def step(S, xs):
        q_i, k_i, w_i, u_i, qk_i, g_i = xs
        v_new = u_i - jnp.einsum('bhck,bhkv->bhcv', w_i, S)
        o = (jnp.einsum('bhck,bhkv->bhcv', q_i * jnp.exp(g_i)[..., None], S)
             + jnp.einsum('bhij,bhjv->bhiv', qk_i, v_new))
        g_last = g_i[..., -1]
        k_dec = k_i * jnp.exp(g_last[..., None] - g_i)[..., None]
        S = S * jnp.exp(g_last)[..., None, None] + jnp.einsum('bhck,bhcv->bhkv', k_dec, v_new)
        return S, o

    s_final, oc = lax.scan(step, s0, (qc, kc, wc, uc, qk, gc))
    o = jnp.moveaxis(oc, (0, 3), (1, 2)).reshape(bsz, L, H, dv)
    return o, s_final

def gated_delta_recurrent(q, k, v, beta, g, s0):
    def step(S, xs):
        q_t, k_t, v_t, b_t, g_t = xs
        S = S * jnp.exp(g_t)[..., None, None]
        kv = jnp.einsum('bhkv,bhk->bhv', S, k_t)
        S = S + jnp.einsum('bhk,bhv->bhkv', k_t, (v_t - kv) * b_t[..., None])
        return S, jnp.einsum('bhkv,bhk->bhv', S, q_t)

    xs = tuple(jnp.moveaxis(t, 1, 0) for t in (q, k, v, beta, g))
    s_final, o = lax.scan(step, s0, xs)
    return jnp.moveaxis(o, 0, 1), s_final

def gated_deltanet(h, s0, conv0, w_in, conv_w, a_log, dt_bias, norm_g, w_out, chunked):
    bsz, L, _ = h.shape
    f32 = jnp.float32
    proj = (h @ w_in).astype(f32)
    o1 = DN_CONV_DIM
    o2 = o1 + DN_VAL_DIM
    o3 = o2 + DN_V_HEADS
    qkv, z, b, a = proj[..., :o1], proj[..., o1:o2], proj[..., o2:o3], proj[..., o3:]
    qkv_c, conv_new = short_conv(qkv, conv0.astype(f32), conv_w.astype(f32))
    q = qkv_c[..., :DN_KEY_DIM].reshape(bsz, L, DN_QK_HEADS, DN_HEAD_K)
    k = qkv_c[..., DN_KEY_DIM:2 * DN_KEY_DIM].reshape(bsz, L, DN_QK_HEADS, DN_HEAD_K)
    v = qkv_c[..., 2 * DN_KEY_DIM:].reshape(bsz, L, DN_V_HEADS, DN_HEAD_V)
    rep = DN_V_HEADS // DN_QK_HEADS
    q = jnp.repeat(l2norm(q), rep, axis=2) * (DN_HEAD_K ** -0.5)
    k = jnp.repeat(l2norm(k), rep, axis=2)
    beta = jax.nn.sigmoid(b)
    g = -jnp.exp(a_log.astype(f32)) * jax.nn.softplus(a + dt_bias.astype(f32))
    if chunked:
        o, s_new = gated_delta_chunked(q, k, v, beta, g, s0.astype(f32))
    else:
        o, s_new = gated_delta_recurrent(q, k, v, beta, g, s0.astype(f32))
    o = rmsnorm(o, norm_g) * jax.nn.silu(z.reshape(bsz, L, DN_V_HEADS, DN_HEAD_V))
    out = o.reshape(bsz, L, DN_VAL_DIM).astype(h.dtype) @ w_out
    return out.astype(h.dtype), s_new, conv_new

def s5_combine(e1, e2):
    a1r, a1i, b1r, b1i = e1
    a2r, a2i, b2r, b2i = e2
    return (a2r * a1r - a2i * a1i, a2r * a1i + a2i * a1r,
            a2r * b1r - a2i * b1i + b2r, a2r * b1i + a2i * b1r + b2i)

def s5_mixer(h, s0_re, s0_im, a_re, a_im, log_dt, b_re, b_im, c_re, c_im, d_skip, w_glu):
    f32 = jnp.float32
    bsz, L, _ = h.shape
    u = h.astype(f32).reshape(bsz, L, S5_GROUPS, S5_GROUP)
    a_re, a_im = a_re.astype(f32), a_im.astype(f32)
    dt = jnp.exp(log_dt.astype(f32))[:, None]
    mag = jnp.exp(a_re * dt)
    lb_re, lb_im = mag * jnp.cos(a_im * dt), mag * jnp.sin(a_im * dt)
    den = a_re * a_re + a_im * a_im
    n_re, n_im = lb_re - 1.0, lb_im
    f_re = (n_re * a_re + n_im * a_im) / den
    f_im = (n_im * a_re - n_re * a_im) / den
    b_re, b_im = b_re.astype(f32), b_im.astype(f32)
    bb_re = f_re[..., None] * b_re - f_im[..., None] * b_im
    bb_im = f_re[..., None] * b_im + f_im[..., None] * b_re
    bu_re = jnp.einsum('gpc,blgc->blgp', bb_re, u)
    bu_im = jnp.einsum('gpc,blgc->blgp', bb_im, u)
    ar = jnp.broadcast_to(lb_re, bu_re.shape)
    ai = jnp.broadcast_to(lb_im, bu_im.shape)
    pr, pi, sr, si = lax.associative_scan(s5_combine, (ar, ai, bu_re, bu_im), axis=1)
    s0_re = s0_re.astype(f32)[:, None]
    s0_im = s0_im.astype(f32)[:, None]
    st_re = sr + pr * s0_re - pi * s0_im
    st_im = si + pr * s0_im + pi * s0_re
    y = (jnp.einsum('gcp,blgp->blgc', c_re.astype(f32), st_re)
         - jnp.einsum('gcp,blgp->blgc', c_im.astype(f32), st_im)
         + d_skip.astype(f32).reshape(S5_GROUPS, S5_GROUP) * u)
    y = jax.nn.gelu(y.reshape(bsz, L, D_MODEL)).astype(h.dtype)
    pg = y @ w_glu
    out = pg[..., :D_MODEL] * jax.nn.sigmoid(pg[..., D_MODEL:])
    return out.astype(h.dtype), st_re[:, -1], st_im[:, -1]

def swiglu(h, w_in, w_out):
    gu = h @ w_in
    return (jax.nn.silu(gu[..., :FFN_HIDDEN]) * gu[..., FFN_HIDDEN:]) @ w_out

def trunk(x, dn_ssm0, dn_conv0, s5_re0, s5_im0, chunked,
          norm_mix_g, norm_ffn_g, final_norm_g,
          w_dn_in, dn_conv_w, dn_a_log, dn_dt_bias, dn_norm_g, w_dn_out,
          s5_a_re, s5_a_im, s5_log_dt, s5_b_re, s5_b_im, s5_c_re, s5_c_im, s5_d, w_s5_glu,
          w_ffn_in, w_ffn_out):
    dn_ssm, dn_conv, s5_re, s5_im = [], [], [], []
    for i in range(DEPTH):
        j = i // N_MIXERS
        hn = rmsnorm(x, norm_mix_g[i])
        if i % N_MIXERS == 0:
            out, s_new, c_new = gated_deltanet(hn, dn_ssm0[j], dn_conv0[j], w_dn_in[j], dn_conv_w[j],
                                               dn_a_log[j], dn_dt_bias[j], dn_norm_g[j], w_dn_out[j], chunked)
            dn_ssm.append(s_new)
            dn_conv.append(c_new)
        else:
            out, re_new, im_new = s5_mixer(hn, s5_re0[j], s5_im0[j], s5_a_re[j], s5_a_im[j], s5_log_dt[j],
                                           s5_b_re[j], s5_b_im[j], s5_c_re[j], s5_c_im[j], s5_d[j], w_s5_glu[j])
            s5_re.append(re_new)
            s5_im.append(im_new)
        x = x + out
        x = x + swiglu(rmsnorm(x, norm_ffn_g[i]), w_ffn_in[i], w_ffn_out[i]).astype(x.dtype)
    return (rmsnorm(x, final_norm_g), jnp.stack(dn_ssm), jnp.stack(dn_conv),
            jnp.stack(s5_re), jnp.stack(s5_im))

def setup_inputs(seed: int = 0) -> dict:
    key = jax.random.key(seed)
    ks = iter(jax.random.split(key, 32))
    f32 = jnp.float32

    def nrm(shape, scale):
        return scale * jax.random.normal(next(ks), shape, f32)

    def unif(shape, lo, hi):
        return jax.random.uniform(next(ks), shape, f32, minval=lo, maxval=hi)

    NA, NB = N_DN_LAYERS, N_S5_LAYERS
    dn_dt = jnp.exp(unif((NA, DN_V_HEADS), math.log(1e-3), math.log(1e-1)))
    n_idx = jnp.arange(S5_STATE, dtype=f32)
    return {
        'x_prompt': nrm((BATCH, SEQ, D_MODEL), 1.0),
        'x_sample': nrm((DEC_BATCH, DEC_SEQ, D_MODEL), 1.0),
        'state_dn_ssm': nrm((NA, DEC_BATCH, DN_V_HEADS, DN_HEAD_K, DN_HEAD_V), 0.5),
        'state_dn_conv': nrm((NA, DEC_BATCH, DN_CONV_W - 1, DN_CONV_DIM), 1.0),
        'state_s5_re': nrm((NB, DEC_BATCH, S5_GROUPS, S5_STATE), 0.1),
        'state_s5_im': nrm((NB, DEC_BATCH, S5_GROUPS, S5_STATE), 0.1),
        'norm_mix_g': 1.0 + nrm((DEPTH, D_MODEL), 0.02),
        'norm_ffn_g': 1.0 + nrm((DEPTH, D_MODEL), 0.02),
        'final_norm_g': 1.0 + nrm((D_MODEL,), 0.02),
        'w_dn_in': nrm((NA, D_MODEL, DN_IN_DIM), D_MODEL ** -0.5),
        'dn_conv_w': nrm((NA, DN_CONV_W, DN_CONV_DIM), DN_CONV_W ** -0.5),
        'dn_a_log': jnp.log(unif((NA, DN_V_HEADS), 1.0, 16.0)),
        'dn_dt_bias': dn_dt + jnp.log(-jnp.expm1(-dn_dt)),
        'dn_norm_g': 1.0 + nrm((NA, DN_HEAD_V), 0.02),
        'w_dn_out': nrm((NA, DN_VAL_DIM, D_MODEL), DN_VAL_DIM ** -0.5),
        's5_a_re': -0.5 + nrm((NB, S5_GROUPS, S5_STATE), 0.01),
        's5_a_im': math.pi * n_idx + nrm((NB, S5_GROUPS, S5_STATE), 0.01),
        's5_log_dt': unif((NB, S5_GROUPS), math.log(1e-3), math.log(1e-1)),
        's5_b_re': nrm((NB, S5_GROUPS, S5_STATE, S5_GROUP), (2 * S5_GROUP) ** -0.5),
        's5_b_im': nrm((NB, S5_GROUPS, S5_STATE, S5_GROUP), (2 * S5_GROUP) ** -0.5),
        's5_c_re': nrm((NB, S5_GROUPS, S5_GROUP, S5_STATE), S5_STATE ** -0.5),
        's5_c_im': nrm((NB, S5_GROUPS, S5_GROUP, S5_STATE), S5_STATE ** -0.5),
        's5_d': nrm((NB, D_MODEL), 1.0),
        'w_s5_glu': nrm((NB, D_MODEL, 2 * D_MODEL), D_MODEL ** -0.5),
        'w_ffn_in': nrm((DEPTH, D_MODEL, 2 * FFN_HIDDEN), D_MODEL ** -0.5),
        'w_ffn_out': nrm((DEPTH, FFN_HIDDEN, D_MODEL), FFN_HIDDEN ** -0.5),
    }

def reference(x_prompt, x_sample, state_dn_ssm, state_dn_conv, state_s5_re, state_s5_im,
              norm_mix_g, norm_ffn_g, final_norm_g,
              w_dn_in, dn_conv_w, dn_a_log, dn_dt_bias, dn_norm_g, w_dn_out,
              s5_a_re, s5_a_im, s5_log_dt, s5_b_re, s5_b_im, s5_c_re, s5_c_im, s5_d, w_s5_glu,
              w_ffn_in, w_ffn_out):
    weights = (norm_mix_g, norm_ffn_g, final_norm_g,
               w_dn_in, dn_conv_w, dn_a_log, dn_dt_bias, dn_norm_g, w_dn_out,
               s5_a_re, s5_a_im, s5_log_dt, s5_b_re, s5_b_im, s5_c_re, s5_c_im, s5_d, w_s5_glu,
               w_ffn_in, w_ffn_out)
    bp = x_prompt.shape[0]
    f32 = jnp.float32
    z_ssm = jnp.zeros((N_DN_LAYERS, bp, DN_V_HEADS, DN_HEAD_K, DN_HEAD_V), f32)
    z_conv = jnp.zeros((N_DN_LAYERS, bp, DN_CONV_W - 1, DN_CONV_DIM), f32)
    z_s5 = jnp.zeros((N_S5_LAYERS, bp, S5_GROUPS, S5_STATE), f32)
    y_prompt, dn_ssm_p, dn_conv_p, s5_re_p, s5_im_p = trunk(
        x_prompt, z_ssm, z_conv, z_s5, z_s5, True, *weights)
    y_sample, dn_ssm_s, dn_conv_s, s5_re_s, s5_im_s = trunk(
        x_sample, state_dn_ssm, state_dn_conv, state_s5_re, state_s5_im, False, *weights)
    return (y_prompt, y_sample, dn_ssm_p, dn_conv_p, s5_re_p, s5_im_p,
            dn_ssm_s, dn_conv_s, s5_re_s, s5_im_s)


_drawn_inputs = setup_inputs


def setup_inputs(seed=0):
    import zlib

    import numpy as np

    out = dict(_drawn_inputs(seed))
    spreads = {}
    factors = {'norm_ffn_g': 3.1,
     'final_norm_g': 8.061,
     'dn_norm_g': 4.467,
     's5_a_re': 15.783,
     's5_c_re': 8.0,
     's5_c_im': 8.0}
    for name, (base, spread) in spreads.items():
        noise = np.random.default_rng([zlib.crc32(name.encode()), seed]).standard_normal(out[name].shape)
        drawn = base * np.exp(spread * noise) if base else spread * noise
        out[name] = __import__('jax').numpy.asarray(drawn.astype(out[name].dtype))
    for name, factor in factors.items():
        out[name] = (out[name] * factor).astype(out[name].dtype)
    return out
```

```python
import math
from contextlib import ExitStack

import numpy as np
import concourse.bass as bass
from concourse import mybir

F32 = mybir.dt.float32
F32R = mybir.dt.float32r
ALU = mybir.AluOpType
AF = mybir.ActivationFunctionType

P = 128
D = 1024
KT = D // P
T = 1024
B = 8
N = T + B
NC3 = 3
NB = N // NC3
HQK, HV = 8, 16
CONVW = 4
FF = 2816
FT = FF // P
UW = KT * P
EPS = 1e-6
CH = 128
QCH = 2
NQ = T // CH // QCH
STEP = 8
NBLK = T // STEP
G16 = 16
NPAIR = 32
PQ = 4
SR = NPAIR // PQ
UC = NBLK + 2 * B
XC = NBLK + B
NVB = -(-PQ // 3)
UNITS_MIX, UNITS_FFN, UNITS_GLU = 8, 6, 2
N_UNITS = 1 + HQK * UNITS_MIX + 2 * (FT // 2) * UNITS_FFN + KT * UNITS_GLU


class Steps:

    def __init__(self, sem, plan, who):
        self.sem, self.plan, self.who = sem, plan, who
        self.base, self.k, self.phase, self.i = 0, 0, None, 0

    def begin(self, phase, i):
        self.phase, self.i, self.k = phase, i, 0

    def end(self, count):
        self.plan[(self.who, self.phase)] = (self.base, self.k, count)
        self.base += self.k * count

    def done(self, ins, name=None):
        ins.then_inc(self.sem, 1)
        self.k += 1
        if name is not None:
            self.plan[(self.who, self.phase, name)] = self.k
        return ins


def build(nc, dr, plan):
    ctx = ExitStack()
    with ctx:
        def sb(name, shape, dt=F32, c=ctx):
            return c.enter_context(nc.sbuf_tensor(name, shape, dt))

        def sem(name):
            return ctx.enter_context(nc.semaphore(name))

        x = sb("x", [P, KT, N])
        hhi = sb("hhi", [P, KT, N], F32R)
        hlo = sb("hlo", [P, KT, N], F32R)
        wtick = sb("wtick", [P, 2])
        wraw = sb("wraw", [P, 2, UW])
        whi = sb("whi", [P, 2, UW], F32R)
        wlo = sb("wlo", [P, 2, UW], F32R)
        ones = sb("ones", [P, P])
        ident = sb("ident", [P, P])
        gains = sb("gains", [P, 5, KT])
        ps = ctx.enter_context(nc.psum_tensor("ps", [P, 8, 512], F32))

        w_loaded = [sem("w_loaded0"), sem("w_loaded1")]
        w_hi = sem("w_hi")
        w_split = sem("w_split")
        w_used = sem("w_used")
        lev_done = sem("lev_done")
        const_ready = sem("const_ready")
        in_x = sem("in_x")
        in_par = sem("in_par")
        in_conv = sem("in_conv")
        in_state = sem("in_state")
        out_small = sem("out_small")
        out_state = sem("out_state")
        u_store = [sem("u_store0"), sem("u_store1")]
        u_load = sem("u_load")
        h_shift = sem("h_shift")
        y_store = sem("y_store")
        y_load = [sem("y_load0"), sem("y_load1")]
        s5_out = sem("s5_out")
        s5_par = sem("s5_par")
        out_y = sem("out_y")
        sems = {"PE": sem("pe_steps"), "ACT": sem("act_steps"), "DVE": sem("dve_steps")}

        unit_base = {}

        class Eng:
            def __init__(self, who, eng):
                self.who, self.e = who, eng
                self.s = Steps(sems[who], plan, who)
                self.i = 0

            def begin(self, phase, i):
                self.i = i
                self.s.begin(phase, i)

            def after(self, who, name, di=0):
                base, per, _ = plan.get((who, self.s.phase), (0, 1, 1))
                k = plan.get((who, self.s.phase, name))
                if k is None:
                    plan["missing"].add((who, self.s.phase, name))
                    k = 1
                self.e.wait_ge(sems[who], self.i * per + (base + k))

            def do(self, ins, name=None):
                self.s.done(ins, name)
                if self.who != "PE":
                    base, per, _ = plan.get((self.who, self.s.phase), (0, 1, 1))
                    self.e.wait_ge(sems[self.who], self.i * per + (base + self.s.k))

            def meet(self):
                for who in sems:
                    base, per, _ = plan.get((who, self.s.phase), (0, 1, 1))
                    if per:
                        self.e.wait_ge(sems[who], (self.i + 1) * per + base)

            def mark(self):
                self.do(nc.scalar.activation(eps_t[:, 1:2], eps_t[:, 0:1], AF.Copy), "marked")

            def unit_done(self, u):
                ph = self.s.phase
                base, per = unit_base[ph]
                self.e.wait_ge(w_used, self.i * per + (base + u + 1))

            def run(self, phase, count, body, c=None):
                if count == 1:
                    self.begin(phase, 0)
                    body(self)
                    self.meet()
                else:
                    with self.e.Fori(0, count) as i:
                        self.begin(phase, i)
                        body(self)
                        self.meet()
                self.s.end(count)

        ub = 0
        for ph, per, cnt in (("prolog", 1, 1), ("mix", UNITS_MIX, HQK), ("ffn0", UNITS_FFN, FT // 2),
                             ("glu", UNITS_GLU, KT), ("ffn1", UNITS_FFN, FT // 2)):
            unit_base[ph] = (ub, per)
            ub += per * cnt
        assert ub == N_UNITS

        def blk(n):
            return slice(n * NB, (n + 1) * NB)

        def wait_weights(p, u):
            base, per = unit_base[p.s.phase]
            p.e.wait_ge(w_split, p.i * per + (base + u + 1))
            return (base + u) % 2

        def project(p, u, triple, name):
            s = wait_weights(p, u)
            for n in range(NC3):
                out = ps[:, 3 * triple + n, 0:NB]
                k = 0
                for kt in range(KT):
                    w_h = whi[:, s, kt * P:(kt + 1) * P]
                    w_l = wlo[:, s, kt * P:(kt + 1) * P]
                    for w, r in ((w_h, hhi), (w_h, hlo), (w_l, hhi)):
                        ins = nc.tensor.matmul(out, w, r[:, kt, blk(n)], start=k == 0, stop=k == 3 * KT - 1)
                        k += 1
                if n < NC3 - 1:
                    p.do(ins, f"{name}{n}")
                else:
                    ins.then_inc(w_used, 1)

        def project_out(p, u, half, rhi, rlo, free):
            s = wait_weights(p, u)
            for mm in range(4):
                m = 4 * half + mm
                free(m)
                for n in range(NC3):
                    out = ps[:, 3 * (m % 2) + n, 0:NB]
                    k = 0
                    for kt in range(2):
                        c = kt * 512 + mm * P
                        for w, r in ((whi, rhi), (whi, rlo), (wlo, rhi)):
                            ins = nc.tensor.matmul(out, w[:, s, c:c + P], r[:, kt, blk(n)], start=k == 0, stop=k == 5)
                            k += 1
                    if mm == 3 and n == NC3 - 1:
                        ins.then_inc(w_used, 1)
                    else:
                        p.do(ins, f"out{m}.{n}")

        def wait_out(v, u0, m, n):
            if m % 4 == 3 and n == NC3 - 1:
                v.unit_done(u0 + m // 4)
            else:
                v.after("PE", f"out{m}.{n}")

        def add_out(v, u0):
            for m in range(KT):
                for n in range(NC3):
                    wait_out(v, u0, m, n)
                    v.do(nc.vector.tensor_tensor(x[:, m, blk(n)], ps[:, 3 * (m % 2) + n, 0:NB], x[:, m, blk(n)], ALU.add), f"x{m}.{n}")

        def norm_pe(p, banks=0):
            for kt in range(KT):
                p.after("ACT", f"sq{kt}")
                for n in range(NC3):
                    ins = nc.tensor.matmul(ps[:, banks + n, 0:NB], ones[:, :], nsq[:, kt % 2, blk(n)], start=kt == 0, stop=kt == KT - 1)
                p.do(ins, f"ss{kt}")

        def norm_act(a):
            for kt in range(KT):
                if kt >= 2:
                    a.after("PE", f"ss{kt - 2}")
                a.do(nc.scalar.activation(nsq[:, kt % 2, :], x[:, kt, :], AF.Square), f"sq{kt}")
            a.after("PE", f"ss{KT - 1}")
            for n in range(NC3):
                a.do(nc.scalar.activation(nr[:, blk(n)], ps[:, n, 0:NB], AF.Sqrt, bias=eps_t[:, 0:1], scale=1.0 / D), "rms")

        def norm_hi(a):
            for kt in range(KT):
                a.after("DVE", f"h{kt}")
                a.do(nc.scalar.activation(hhi[:, kt, :], nh[:, kt % 2, :], AF.Copy), f"hi{kt}")

        def norm_dve(v, gi):
            v.e.wait_ge(in_par, 16 * 4)
            v.after("ACT", "rms")
            v.do(nc.vector.reciprocal(nr[:, :], nr[:, :]), "rr")
            for kt in range(KT + 1):
                if kt < KT:
                    v.do(nc.vector.scalar_tensor_tensor(nh[:, kt % 2, :], x[:, kt, :], gains[:, gi, kt:kt + 1], nr[:, :], ALU.mult, ALU.mult), f"h{kt}")
                if kt >= 1:
                    v.after("ACT", f"hi{kt - 1}")
                    v.do(nc.vector.tensor_tensor(hlo[:, kt - 1, :], nh[:, (kt - 1) % 2, :], hhi[:, kt - 1, :].bitcast(F32), ALU.subtract), f"lo{kt - 1}")

        eps_t = sb("eps_t", [P, 4])

        mixc = ctx.enter_context(ExitStack())
        mix = {}

        def m_(name, shape):
            mix[name] = sb(name, shape, F32, mixc)
            return mix[name]

        pre = m_("pre", [P, 2, 3 + N])
        qkv = m_("qkv", [P, 4, N])
        sq = m_("sq", [P, N])
        upin = m_("upin", [P, P])
        slow = m_("slow", [P, P])
        lev = m_("lev", [P, 8, P])
        dwork = m_("dwork", [P, 11, 4, P])
        ktok = m_("ktok", [P, QCH, P])
        vnew = m_("vnew", [P, 2, P])
        S = m_("S", [P, 2, P])
        ohi = sb("ohi", [P, 2, N], F32R, mixc)
        olo = sb("olo", [P, 2, N], F32R, mixc)
        tabs = m_("tabs", [P, 6, KT, HV])
        stab = m_("stab", [P, 2, HV, B])
        tg = m_("tg", [P, 6, 2, KT])
        cw = m_("cw", [P, HQK, 4, CONVW])
        cst = m_("cst", [P, 4, 3, B])
        cso = m_("cso", [P, 4, 3, B])
        cpo = m_("cpo", [P, 4, 3])
        ng = m_("ng", [P, 1])
        sdel = m_("sdel", [P, 6, 2, B])
        GSL, GU, EXPD, EG, TT_, NT, YY, ATT, KD, KB, VB = (dwork[:, i] for i in range(11))
        NM, PP, NWT = GSL, GU, EXPD
        S0 = dwork[:, 4:8].rearrange("p a b c -> p (a b) c")
        nsq = qkv[:, 0:2]
        nr = sq
        nh = qkv[:, 2:4]
        ba = pre[:, 0, 0:N]
        rec = dwork[:, 0:3].rearrange("p a b c -> p (a b c)")[:, 0:N]
        bst = dwork[:, 0:8].rearrange("p a b c -> p a (b c)")

        def pro_pe(p):
            p.e.wait_ge(const_ready, 1)
            norm_pe(p)
            p.after("DVE", f"lo{KT - 1}")
            project(p, 0, 1, "ba")
            p.after("ACT", "ba")
            p.e.wait_ge(const_ready, 6)
            for c in range(KT):
                ins = nc.tensor.transpose(ps[:, 0, c * 32:(c + 1) * 32], ba[0:32, c * P:(c + 1) * P], ident[0:32, 0:32])
            ins = nc.tensor.transpose(ps[0:B, 1, 0:32], ba[0:32, T:N], ident[0:32, 0:32])
            p.do(ins, "bat")
            p.after("DVE", "g")
            nc.tensor.matmul(ps[:, 2, 0:128], upin[:, :], tabs[:, 1].rearrange("p c h -> p (c h)"), start=True, stop=True)
            nc.tensor.matmul(ps[:, 2, 128:256], slow[:, :], tabs[:, 1].rearrange("p c h -> p (c h)"), start=True, stop=True)
            nc.tensor.matmul(ps[:, 2, 256:384], ones[:, :], tabs[:, 1].rearrange("p c h -> p (c h)"), start=True, stop=True)
            p.do(nc.tensor.matmul(ps[:, 3, 0:256], ones[0:B, :], bst[0:B, 7, 0:256], start=True, stop=True), "cum")

        def pro_act(a):
            a.e.wait_ge(in_x, 16)
            a.e.wait_ge(const_ready, 1)
            norm_act(a)
            norm_hi(a)
            for n in range(NC3):
                if n < 2:
                    a.after("PE", f"ba{n}")
                else:
                    a.unit_done(0)
                a.do(nc.scalar.activation(ba[:, blk(n)], ps[:, 3 + n, 0:NB], AF.Copy), "ba")
            a.after("DVE", "z")
            a.e.wait_ge(in_par, 16 * 4)
            a.do(nc.scalar.activation(bst[:, 1, :], bst[:, 0, :], AF.Exp, scale=-1.0), "eb")
            a.do(nc.scalar.activation(bst[:, 3, :], bst[:, 3, :], AF.Exp, scale=-1.0), "ez")
            a.do(nc.scalar.activation(bst[:, 5, 0:HV], alog[:, 0, :], AF.Exp), "ea")
            a.do(nc.scalar.activation(bst[:, 3, :], bst[:, 3, :], AF.Ln, bias=1.0), "ln")
            a.after("PE", "cum")
            a.do(nc.scalar.activation(tabs[:, 2:5].rearrange("p t c h -> p (t c h)"), ps[:, 2, 0:384], AF.Exp), "tab")
            a.do(nc.scalar.activation(stab[:, 0].rearrange("p h b -> p (h b)"), ps[:, 3, 0:128], AF.Exp), "stab")

        def pro_dve(v):
            norm_dve(v, 0)
            V = nc.vector
            v.after("PE", "bat")
            nb_ = KT * HV
            v.e.wait_ge(in_par, 16 * 4)
            for t in range(2):
                src = ps[:, 0, 0:256].rearrange("p (c f) -> p c f", f=32)[:, :, 16 * t:16 * t + 16]
                v.do(V.tensor_copy(bst[:, 2 * t, 0:nb_].rearrange("p (c h) -> p c h", h=HV), src))
                v.do(V.memset(bst[:, 2 * t, nb_:512], 0.0))
                v.do(V.tensor_copy(bst[0:B, 2 * t, nb_:nb_ + 16], ps[0:B, 1, 16 * t:16 * t + 16]))
            zz = bst[:, 2, 0:nb_ + 16].rearrange("p (c h) -> p c h", h=HV)
            v.do(V.tensor_tensor(zz, zz, alog[:, 1, :].unsqueeze(1).to_broadcast([P, KT + 1, HV]), ALU.add))
            v.do(V.tensor_scalar(bst[:, 4, :], bst[:, 2, :], -1.0, None, ALU.mult))
            v.do(V.tensor_tensor(bst[:, 3, :], bst[:, 2, :], bst[:, 4, :], ALU.max), "z")
            v.do(V.tensor_scalar(bst[:, 4, :], bst[:, 2, :], 0.0, None, ALU.max))
            v.after("ACT", "eb")
            v.do(V.tensor_scalar(bst[:, 1, :], bst[:, 1, :], 1.0, None, ALU.add))
            v.do(V.reciprocal(bst[:, 1, :], bst[:, 1, :]))
            v.after("ACT", "ln")
            v.do(V.tensor_tensor(bst[:, 3, :], bst[:, 3, :], bst[:, 4, :], ALU.add))
            g3 = bst[:, 3, 0:nb_ + 16].rearrange("p (c h) -> p c h", h=HV)
            v.do(V.scalar_tensor_tensor(g3, g3, -1.0, bst[:, 5, 0:HV].unsqueeze(1).to_broadcast([P, KT + 1, HV]), ALU.mult, ALU.mult))
            flat = lambda a_: a_.rearrange("p c h -> p (c h)")
            v.do(V.tensor_copy(flat(tabs[:, 0]), bst[:, 1, 0:nb_]))
            for j, s_ in ((0, 3), (1, 1)):
                i0 = bst[0:B, s_, nb_:nb_ + 16].unsqueeze(2).to_broadcast([B, HV, B])
                i1 = ident[0:B, 0:B].unsqueeze(1).to_broadcast([B, HV, B])
                v.do(V.tensor_tensor(bst[0:B, 7, 128 * j:128 * j + 128].rearrange("p (h b) -> p h b", b=B), i0, i1, ALU.mult))
            v.do(V.tensor_copy(flat(tabs[:, 1]), bst[:, 3, 0:nb_]), "g")
            v.after("ACT", "stab")
            v.do(V.tensor_tensor(flat(tabs[:, 5]), flat(tabs[:, 0]), flat(tabs[:, 2]), ALU.mult))
            v.do(V.tensor_copy(stab[:, 1].rearrange("p h b -> p (h b)"), ps[:, 3, 128:256]))
            v.do(V.memset(pre[:, :, 0:3], 0.0))

        alog = m_("alog", [P, 2, HV])

        CONV = ["k", "q", "v0", "v1"]

        def mix_pe(p):
            for t, nm in enumerate(CONV):
                if t >= 2:
                    p.after("ACT", f"pre{t - 2}")
                project(p, t, t % 2, f"c{t}.")
            for j in range(2):
                p.after("ACT", f"pre{2 + j}")
                p.after("DVE", f"sq{j}")
                for n in range(NC3):
                    ins = nc.tensor.matmul(ps[:, 3 * j + n, 0:NB], ones[:, :], sq[:, blk(n)], start=True, stop=True)
                p.do(ins, f"nk{j}")
            for qd in range(NQ):
                q_ = f"q{qd}."
                ch = [slice((QCH * qd + c) * CH, (QCH * qd + c + 1) * CH) for c in range(QCH)]
                p.after("DVE", "qn" if qd == 0 else f"q{qd - 1}.S{QCH - 1}.1")
                if qd:
                    p.after("ACT", f"q{qd - 1}.o{QCH - 1}.1")
                for c in range(QCH):
                    nc.tensor.matmul(ps[:, 0, c * P:(c + 1) * P], qkv[:, 0, ch[c]], qkv[:, 0, ch[c]], start=True, stop=True)
                    ins = nc.tensor.matmul(ps[:, 0, 256 + c * P:256 + (c + 1) * P], qkv[:, 1, ch[c]], qkv[:, 0, ch[c]], start=True, stop=True)
                p.do(ins, q_ + "G")
                for c in range(QCH):
                    ins = nc.tensor.transpose(ps[:, 1, c * P:(c + 1) * P], qkv[:, 0, ch[c]], ident[:, :])
                p.do(ins, q_ + "kT")
                if qd == 0:
                    p.after("ACT", "silu3")
                for h in range(2):
                    for c in range(QCH):
                        ins = nc.tensor.transpose(ps[:, 2, (2 * h + c) * P:(2 * h + c + 1) * P], qkv[:, 2 + h, ch[c]], ident[:, :])
                p.do(ins, q_ + "vT")
                p.after("DVE", q_ + "gsl")
                p.do(nc.tensor.matmul(ps[:, 3, :], upin[:, :], GSL.rearrange("p a b -> p (a b)"), start=True, stop=True), q_ + "diff")
                p.after("DVE", q_ + "gu")
                p.do(nc.tensor.matmul(ps[:, 4, :], ones[:, :], GU.rearrange("p a b -> p (a b)"), start=True, stop=True), q_ + "eg")
                p.after("DVE", q_ + "L")
                for j in range(4):
                    ins = nc.tensor.transpose(ps[:, 5, j * P:(j + 1) * P], TT_[:, j], ident[:, :])
                p.do(ins, q_ + "LT")
                p.after("DVE", q_ + "attn")
                for j in range(4):
                    ins = nc.tensor.transpose(ps[:, 6, j * P:(j + 1) * P], EXPD[:, j], ident[:, :])
                p.do(ins, q_ + "aT")
                for l in range(1, 7):
                    for h in range(2):
                        p.after("DVE", q_ + (f"Y{l - 1}.{h}" if l > 1 else "Y0"))
                        p.after("DVE", q_ + f"NM{l}.{h}")
                        for c in range(QCH):
                            j = 2 * h + c
                            ins = nc.tensor.matmul(ps[:, h, c * P:(c + 1) * P], NM[:, j], TT_[:, j], start=True, stop=True)
                        p.do(ins, q_ + f"P{l}.{h}")
                    for h in range(2):
                        p.after("ACT", q_ + f"P{l}.{h}")
                        if l < 6:
                            for c in range(QCH):
                                j = 2 * h + c
                                ins = nc.tensor.matmul(ps[:, 2 + h, c * P:(c + 1) * P], YY[:, j], PP[:, j], start=True, stop=True)
                            p.do(ins, q_ + f"TP{l}.{h}")
                        for c in range(QCH):
                            j = 2 * h + c
                            ins = nc.tensor.matmul(ps[:, 4 + h, c * P:(c + 1) * P], PP[:, j], YY[:, j], start=True, stop=True)
                        p.do(ins, q_ + f"PY{l}.{h}")
                for h in range(2):
                    p.after("DVE", q_ + f"Y6.{h}")
                    for c in range(QCH):
                        j = 2 * h + c
                        ins = nc.tensor.matmul(ps[:, 6, j * P:(j + 1) * P], KB[:, j], YY[:, j], start=True, stop=True)
                p.do(ins, q_ + "wT")
                p.after("ACT", q_ + "nwT")
                for c in range(QCH):
                    for h in range(2):
                        j = 2 * h + c
                        nc.tensor.matmul(ps[:, h, 0:P], YY[:, j], VB[:, j], start=True, stop=False)
                        if c:
                            p.after("DVE", q_ + f"S{c - 1}.{h}")
                        p.do(nc.tensor.matmul(ps[:, h, 0:P], NWT[:, j], S[:, h], start=False, stop=True), q_ + f"vn{c}.{h}")
                    for h in range(2):
                        j = 2 * h + c
                        if c:
                            p.after("ACT", q_ + f"o{c - 1}.{h}")
                        nc.tensor.matmul(ps[:, 2 + h, 0:P], S[:, h], EG[:, j], start=True, stop=False)
                        p.after("ACT", q_ + f"vn{c}.{h}")
                        p.do(nc.tensor.matmul(ps[:, 2 + h, 0:P], vnew[:, h], ATT[:, j], start=False, stop=True), q_ + f"o{c}.{h}")
                        p.do(nc.tensor.matmul(ps[:, 4 + h, 0:P], KD[:, j], vnew[:, h], start=True, stop=True), q_ + f"S{c}.{h}")
            p.after("DVE", f"q{NQ - 1}.S{QCH - 1}.1")
            p.after("ACT", f"q{NQ - 1}.o{QCH - 1}.1")
            for t in range(2):
                project(p, 4 + t, t, f"z{t}.")
            p.e.wait_ge(in_state, p.i * 16 + 16)
            for j in range(16):
                ins = nc.tensor.matmul(ps[:, 6, 2 * j:2 * j + 2], S0[:, j], qkv[:, 0:2, T + j % B], start=True, stop=True)
            p.after("DVE", "kq")
            p.do(nc.tensor.matmul(ps[:, 6, 64:64 + B], ones[:, :], sdel[:, 0, 0], start=True, stop=True), "S0kq")
            p.after("DVE", "delta")
            p.after("ACT", "z1")
            for j in range(16):
                ins = nc.tensor.matmul(ps[:, j // 4, (j % 4) * P:(j % 4 + 1) * P], sdel[:, 1, j // B, j % B:j % B + 1].to_broadcast([P, P]), ident[:, :], start=True, stop=True)
            p.do(ins, "drow")
            for h in range(2):
                p.after("DVE", f"osq{h}")
                p.after("DVE", "snew")
                for n in range(NC3):
                    ins = nc.tensor.matmul(ps[:, 3 * h + n, 0:NB], ones[:, :], sq[:, blk(n)], start=True, stop=True)
                p.do(ins, f"no{h}")
            p.after("ACT", "or1")
            p.after("DVE", "olo1")

            def free(m):
                if m >= 2:
                    p.after("DVE", f"x{m - 2}.{NC3 - 1}")
            project_out(p, 6, 0, ohi, olo, free)
            project_out(p, 7, 1, ohi, olo, free)

        def mix_act(a):
            A = nc.scalar
            gi = a.i

            def evac(t):
                if t >= 2:
                    a.after("DVE", f"conv{t - 2}")
                for n in range(NC3):
                    if n < 2:
                        a.after("PE", f"c{t}.{n}")
                    else:
                        a.unit_done(t)
                    a.do(A.activation(pre[:, t % 2, 3 + n * NB:3 + (n + 1) * NB], ps[:, 3 * (t % 2) + n, 0:NB], AF.Copy), f"pre{t}")

            def silu(t):
                a.after("DVE", f"conv{t}")
                a.do(A.activation(qkv[:, t, :], qkv[:, t, :], AF.Silu), f"silu{t}")

            evac(0)
            evac(1)
            silu(0)
            evac(2)
            silu(1)
            evac(3)
            silu(2)
            silu(3)
            A.dma_start(dr["cso"][gi], cso[:, :, :, :]).then_inc(out_small, 16)
            A.dma_start(dr["cpo"][gi], cpo[:, :, :]).then_inc(out_small, 16)
            for j in range(2):
                a.after("PE", f"nk{j}")
                for n in range(NC3):
                    a.do(A.activation(sq[:, blk(n)], ps[:, 3 * j + n, 0:NB], AF.Sqrt, bias=eps_t[:, 0:1]), f"nr{j}")
            for qd in range(NQ):
                q_ = f"q{qd}."
                a.after("PE", q_ + "kT")
                a.do(A.activation(ktok[:, :, :].rearrange("p a b -> p (a b)"), ps[:, 1, 0:256], AF.Copy), q_ + "ktok")
                a.after("PE", q_ + "diff")
                a.do(A.activation(EXPD.rearrange("p a b -> p (a b)"), ps[:, 3, :], AF.Exp), q_ + "expd")
                a.after("PE", q_ + "eg")
                a.do(A.activation(EG.rearrange("p a b -> p (a b)"), ps[:, 4, :], AF.Exp), q_ + "eg")
                a.after("PE", q_ + "LT")
                a.do(A.activation(NT.rearrange("p a b -> p (a b)"), ps[:, 5, :], AF.Copy), q_ + "NT")
                for l in range(1, 7):
                    for h in range(2):
                        a.after("PE", q_ + f"P{l}.{h}")
                        a.do(A.activation(PP[:, 2 * h:2 * h + 2].rearrange("p a b -> p (a b)"), ps[:, h, 0:256], AF.Copy), q_ + f"P{l}.{h}")
                a.after("PE", q_ + "wT")
                a.do(A.activation(NWT.rearrange("p a b -> p (a b)"), ps[:, 6, :], AF.Copy, scale=-1.0), q_ + "nwT")
                for c in range(QCH):
                    for h in range(2):
                        a.after("PE", q_ + f"vn{c}.{h}")
                        a.do(A.activation(vnew[:, h], ps[:, h, 0:P], AF.Copy), q_ + f"vn{c}.{h}")
                    for h in range(2):
                        a.after("PE", q_ + f"o{c}.{h}")
                        cc = QCH * qd + c
                        a.do(A.activation(qkv[:, 2 + h, cc * CH:(cc + 1) * CH], ps[:, 2 + h, 0:P], AF.Copy), q_ + f"o{c}.{h}")
            a.after("DVE", f"q{NQ - 1}.S{QCH - 1}.1")
            A.dma_start(S0, dr["sin"][gi]).then_inc(in_state, 16)
            A.dma_start(dr["sp"][gi], S[:, :, :]).then_inc(out_small, 16)
            for t in range(2):
                for n in range(NC3):
                    if n < 2:
                        a.after("PE", f"z{t}.{n}")
                    else:
                        a.unit_done(4 + t)
                    a.do(A.activation(pre[:, t, blk(n)], ps[:, 3 * t + n, 0:NB], AF.Silu), f"z{t}")
            a.after("DVE", "snew")
            A.dma_start(dr["sout"][gi], S0).then_inc(out_state, 16)
            for h in range(2):
                a.after("PE", f"no{h}")
                for n in range(NC3):
                    a.do(A.activation(sq[:, blk(n)], ps[:, 3 * h + n, 0:NB], AF.Sqrt, bias=eps_t[:, 0:1], scale=1.0 / P), f"or{h}")
                a.after("DVE", f"og{h}")
                a.do(A.activation(ohi[:, h, :], qkv[:, 2 + h, :], AF.Copy), f"ohi{h}")
            a.e.wait_ge(out_state, a.i * 16 + 16)
            a.e.wait_ge(out_small, a.i * 48 + 48)
            a.mark()

        def mix_dve(v):
            V = nc.vector
            gi = v.i
            for t_ in range(6):
                src = tabs[:, t_].rearrange("p c (g h) -> p g h c", h=2)
                v.do(V.tensor_copy(tg[:, t_], src[:, bass.ds(gi, 1)].rearrange("p a h c -> p (a h) c")), "tg")
            v.do(V.tensor_copy(sdel[:, 4:6], stab[:, :, :, :].rearrange("p t (g h) b -> p t g h b", h=2)[:, :, bass.ds(gi, 1)].rearrange("p t a h b -> p t (a h) b")), "tg")
            v.do(V.tensor_copy(tcw[:, :, :], cw[:, bass.ds(gi, 1)].rearrange("p a t w -> p (a t) w")))
            v.do(V.memset(S[:, :, :], 0.0))

            def conv(t):
                v.after("ACT", f"pre{t}")
                w = tcw[:, t]
                o = qkv[:, t, 0:T]
                os_ = qkv[:, t, T:N]
                v.do(V.tensor_scalar(o, pre[:, t % 2, 0:T], w[:, 0:1], None, ALU.mult))
                v.do(V.tensor_scalar(os_, pre[:, t % 2, 3 + T:3 + N], w[:, 3:4], None, ALU.mult))
                for j in range(1, 4):
                    v.do(V.scalar_tensor_tensor(o, pre[:, t % 2, j:j + T], w[:, j:j + 1], o, ALU.mult, ALU.add))
                    v.do(V.scalar_tensor_tensor(os_, cst[:, t, j - 1], w[:, j - 1:j], os_, ALU.mult, ALU.add))
                v.do(V.tensor_copy(cpo[:, t], pre[:, t % 2, T:T + 3]))
                v.do(V.tensor_copy(cso[:, t, 0:2], cst[:, t, 1:3]))
                v.do(V.tensor_copy(cso[:, t, 2], pre[:, t % 2, 3 + T:3 + N]), f"conv{t}")

            v.e.wait_ge(in_conv, v.i * 16 + 16)
            conv(0)
            conv(1)
            conv(2)
            v.after("ACT", "silu0")
            v.do(V.tensor_tensor(sq[:, :], qkv[:, 0, :], qkv[:, 0, :], ALU.mult), "sq0")
            conv(3)
            for j in range(2):
                v.after("ACT", f"nr{j}")
                v.do(V.reciprocal(rec, sq[:, :]))
                if j == 0:
                    v.after("ACT", "silu1")
                    v.do(V.tensor_tensor(sq[:, :], qkv[:, 1, :], qkv[:, 1, :], ALU.mult), "sq1")
                v.do(V.scalar_tensor_tensor(qkv[:, j, :], qkv[:, j, :], 1.0 if j == 0 else float(P) ** -0.5, rec, ALU.mult, ALU.mult), "qn")
            tb = lambda t_, c0: tg[:, t_, :, c0:c0 + QCH]
            f4 = lambda a_: a_.rearrange("p (h c) n -> p h c n", c=QCH)
            for qd in range(NQ):
                q_ = f"q{qd}."
                c0 = QCH * qd

                def bc(t_):
                    return [tg[:, t_, h, c0:c0 + QCH].unsqueeze(2).to_broadcast([P, QCH, P]) for h in range(2)]
                if qd:
                    v.after("PE", f"q{qd - 1}.S{QCH - 1}.1")
                for tab, m, dst, nm in ((1, slow, GSL, "gsl"), (1, upin, GU, "gu")):
                    g2 = bc(tab)
                    for h in range(2):
                        v.do(V.tensor_tensor(dst[:, 2 * h:2 * h + 2], g2[h], m[:, :].unsqueeze(1).to_broadcast([P, QCH, P]), ALU.mult), q_ + nm)
                v.after("ACT", q_ + "eg")
                for h in range(2):
                    for c in range(QCH):
                        j = 2 * h + c
                        v.do(V.scalar_tensor_tensor(TT_[:, j], ps[:, 0, c * P:(c + 1) * P], tg[:, 0, h, c0 + c:c0 + c + 1], EXPD[:, j], ALU.mult, ALU.mult), q_ + "L")
                for h in range(2):
                    v.do(V.tensor_tensor(EXPD[:, 2 * h:2 * h + 2], ps[:, 0, 256:512].rearrange("p (c n) -> p c n", n=P), EXPD[:, 2 * h:2 * h + 2], ALU.mult), q_ + "attn")
                v.after("PE", q_ + "vT")
                for h in range(2):
                    v.do(V.tensor_tensor(VB[:, 2 * h:2 * h + 2], ps[:, 2, 256 * h:256 * h + 256].rearrange("p (c n) -> p c n", n=P), bc(0)[h], ALU.mult), q_ + "vb")
                v.after("ACT", q_ + "NT")
                v.do(V.tensor_tensor(YY, NT, lev[:, 1].unsqueeze(1).to_broadcast([P, 4, P]), ALU.mult))
                v.do(V.tensor_tensor(TT_, TT_, lev[:, 0].unsqueeze(1).to_broadcast([P, 4, P]), ALU.mult))
                idb = ident[:, :].unsqueeze(1).to_broadcast([P, 4, P])
                v.do(V.tensor_tensor(TT_, TT_, idb, ALU.add))
                v.do(V.tensor_tensor(YY, YY, idb, ALU.add), q_ + "Y0")

                def nm_(l, h):
                    if l > 1:
                        v.after("PE", q_ + f"P{l - 1}.{h}")
                    v.do(V.tensor_tensor(NM[:, 2 * h:2 * h + 2], NT[:, 2 * h:2 * h + 2], lev[:, 1 + l].unsqueeze(1).to_broadcast([P, 2, P]), ALU.mult), q_ + f"NM{l}.{h}")
                v.after("PE", q_ + "diff")
                nm_(1, 0)
                nm_(1, 1)
                v.after("PE", q_ + "aT")
                v.do(V.tensor_tensor(ATT, ps[:, 6, :].rearrange("p (a b) -> p a b", b=P), upin[:, :].unsqueeze(1).to_broadcast([P, 4, P]), ALU.mult), q_ + "ATT")
                for h in range(2):
                    v.do(V.tensor_tensor(KB[:, 2 * h:2 * h + 2], ktok[:, :, :], bc(5)[h], ALU.mult), q_ + "kb")
                    v.do(V.tensor_tensor(KD[:, 2 * h:2 * h + 2], ktok[:, :, :], bc(3)[h], ALU.mult))
                    v.do(V.tensor_tensor(EG[:, 2 * h:2 * h + 2], EG[:, 2 * h:2 * h + 2], qkv[:, 1, c0 * CH:(c0 + QCH) * CH].rearrange("p (c n) -> p c n", n=P), ALU.mult), q_ + "qg")
                for l in range(1, 7):
                    if l < 6:
                        nm_(l + 1, 0)
                        nm_(l + 1, 1)
                    for h in range(2):
                        if l < 6:
                            v.after("PE", q_ + f"PY{l}.{h}")
                            v.do(V.tensor_tensor(TT_[:, 2 * h:2 * h + 2], ps[:, 2 + h, 0:256].rearrange("p (c n) -> p c n", n=P), TT_[:, 2 * h:2 * h + 2], ALU.add))
                        v.after("PE", q_ + f"PY{l}.{h}")
                        v.do(V.tensor_tensor(YY[:, 2 * h:2 * h + 2], ps[:, 4 + h, 0:256].rearrange("p (c n) -> p c n", n=P), YY[:, 2 * h:2 * h + 2], ALU.add), q_ + f"Y{l}.{h}")
                for c in range(QCH):
                    for h in range(2):
                        v.after("PE", q_ + f"S{c}.{h}")
                        v.do(V.scalar_tensor_tensor(S[:, h], S[:, h], tg[:, 4, h, c0 + c:c0 + c + 1], ps[:, 4 + h, 0:P], ALU.mult, ALU.add), q_ + f"S{c}.{h}")
            ks, qs = qkv[:, 0, T:N], qkv[:, 1, T:N]
            v.do(V.tensor_tensor(sdel[:, 0, 0], ks, qs, ALU.mult), "kq")
            v.after("PE", "S0kq")
            kv = ps[:, 6, 0:32].rearrange("p (h b t) -> p h b t", b=B, t=2)
            vs = qkv[:, 2:4, T:N]
            v.do(V.tensor_tensor(sdel[:, 1], kv[:, :, :, 0], sdel[:, 4], ALU.mult))
            v.do(V.tensor_tensor(sdel[:, 1], vs, sdel[:, 1], ALU.subtract))
            v.do(V.tensor_tensor(sdel[:, 1], sdel[:, 1], sdel[:, 5], ALU.mult), "delta")
            v.do(V.tensor_tensor(sdel[:, 2], kv[:, :, :, 1], sdel[:, 4], ALU.mult))
            v.do(V.tensor_tensor(sdel[:, 3], ps[:, 6, 64:64 + B].unsqueeze(1).to_broadcast([P, 2, B]), sdel[:, 1], ALU.mult))
            v.do(V.tensor_tensor(vs, sdel[:, 2], sdel[:, 3], ALU.add), "so")
            v.e.wait_ge(in_state, v.i * 16 + 16)
            v.do(V.tensor_tensor(S0, S0, sdel[:, 4].rearrange("p h b -> p (h b)").unsqueeze(2).to_broadcast([P, 16, P]), ALU.mult))
            v.after("PE", "drow")
            for j in range(16):
                v.do(V.scalar_tensor_tensor(S0[:, j], ps[:, j // 4, (j % 4) * P:(j % 4 + 1) * P], qkv[:, 0, T + j % B:T + j % B + 1], S0[:, j], ALU.mult, ALU.add), "snew")
            for h in range(2):
                o = qkv[:, 2 + h, :]
                if h == 0:
                    v.after("ACT", f"q{NQ - 1}.o{QCH - 1}.1")
                v.do(V.tensor_tensor(sq[:, :], o, o, ALU.mult), f"osq{h}")
                v.after("ACT", f"or{h}")
                v.do(V.reciprocal(rec, sq[:, :]))
                v.do(V.scalar_tensor_tensor(o, o, ng[:, 0:1], rec, ALU.mult, ALU.mult))
                v.after("ACT", f"z{h}")
                v.do(V.tensor_tensor(o, o, pre[:, h, 0:N], ALU.mult), f"og{h}")
                v.after("ACT", f"ohi{h}")
                v.do(V.tensor_tensor(olo[:, h, :], o, ohi[:, h, :].bitcast(F32), ALU.subtract), f"olo{h}")
            v.do(V.memset(pre[:, :, 0:3], 0.0))
            add_out(v, 6)

        tcw = m_("tcw", [P, 4, CONVW])

        def alloc_ffn(tag, c):
            r = {}
            r["sg"], r["ab"] = sg, ab
            r["ahi"] = sb("ahi" + tag, [P, 2, N], F32R, c)
            r["alo"] = sb("alo" + tag, [P, 2, N], F32R, c)
            return r

        def ffn_pe(r):
            def body(p):
                for f in range(2):
                    for t in range(2):
                        if f:
                            p.after("DVE", f"ab0.{NC3 - 1}")
                        project(p, 2 * f + t, t, f"f{2 * f + t}.")
                p.after("DVE", "alo1")

                def free(m):
                    if m >= 2:
                        p.after("DVE", f"x{m - 2}.{NC3 - 1}")
                    else:
                        p.after("DVE", f"ab1.{NC3 - 1}")
                project_out(p, 4, 0, r["ahi"], r["alo"], free)
                project_out(p, 5, 1, r["ahi"], r["alo"], free)
            return body

        def ffn_act(r):
            def body(a):
                for f in range(2):
                    for n in range(NC3):
                        if n < 2:
                            a.after("PE", f"f{2 * f}.{n}")
                        else:
                            a.unit_done(2 * f)
                        a.do(nc.scalar.activation(r["sg"][:, f, blk(n)], ps[:, n, 0:NB], AF.Silu), f"sg{f}.{n}")
                    a.after("DVE", f"ab{f}.{NC3 - 1}")
                    a.do(nc.scalar.activation(r["ahi"][:, f, :], r["ab"][:, f, :], AF.Copy), f"ahi{f}")
            return body

        def ffn_dve(r):
            def body(v):
                for f in range(2):
                    for n in range(NC3):
                        if n < 2:
                            v.after("PE", f"f{2 * f + 1}.{n}")
                        else:
                            v.unit_done(2 * f + 1)
                        v.after("ACT", f"sg{f}.{n}")
                        v.do(nc.vector.tensor_tensor(r["ab"][:, f, blk(n)], ps[:, 3 + n, 0:NB], r["sg"][:, f, blk(n)], ALU.mult), f"ab{f}.{n}")
                    v.after("ACT", f"ahi{f}")
                    v.do(nc.vector.tensor_tensor(r["alo"][:, f, :], r["ab"][:, f, :], r["ahi"][:, f, :].bitcast(F32), ALU.subtract), f"alo{f}")
                add_out(v, 4)
            return body

        S5 = {}

        mixc.close()

        sg = sb("sg", [P, 2, N])
        ab = sb("ab", [P, 2, N])
        n_sq, n_r, n_h = sg, sb("n_r", [P, N]), ab
        ffc = ExitStack()
        rf = alloc_ffn("", ffc)
        ffc.close()

        s5c = ctx.enter_context(ExitStack())

        def s_(name, shape):
            S5[name] = sb(name, shape, F32, s5c)
            return S5[name]

        hs = s_("hs", [P, 2, N])
        par = s_("par", [P, 3, NPAIR])
        sc = s_("sc", [P, 24, NPAIR])
        lam = s_("lam", [P, 2, 9, NPAIR])
        bq = s_("bq", [P, 2, PQ, G16])
        cq = s_("cq", [P, 2, PQ, G16])
        cp = s_("cp", [P, 2, PQ, 9, G16])
        bp = s_("bp", [P, 2, PQ, STEP, G16])
        t1 = s_("t1", [P, PQ, 9 * G16])
        bbq = s_("bbq", [P, 2, PQ, G16])
        wt = s_("wt", [P, 2, PQ, P])
        kpad = s_("kpad", [G16, 2 * PQ, (2 * STEP - 1) * G16])
        ht = s_("ht", [P, 2 * PQ, P])
        uu = s_("uu", [P, 2 * PQ, UC])
        vv = s_("vv", [P, 2, PQ, UC])
        ee = s_("ee", [P, 2, PQ, NBLK])
        t2 = s_("t2", [P, 2, PQ, NBLK])
        xp = s_("xp", [P, 2, PQ, XC])
        sto = s_("sto", [P, 2, PQ, 1 + B])
        ysmp = s_("ysmp", [G16, 2 * PQ, B])
        pw = s_("pw", [P, 4, 2, PQ])
        s5c.close()
        gelc = ExitStack()
        yf = sb("yf", [P, 2, N], F32, gelc)
        hd = sb("hd", [P, 2, N], F32, gelc)
        dsk = sb("dsk", [P, KT], F32, gelc)
        yg = sb("yg", [P, 2, N], F32, gelc)
        gelc.close()

        def norm_s5_dve(v):
            V = nc.vector
            v.after("ACT", "rms")
            v.do(V.reciprocal(n_r[:, :], n_r[:, :]))
            for kt in range(KT):
                if kt >= 2:
                    v.e.wait_ge(u_store[kt % 2], 16 * (kt // 2))
                for c0, c1 in ((0, T), (T, N)):
                    if c0 == 0:
                        o = hs[:, kt % 2, 0:T].rearrange("p (j c) -> p c j", j=STEP)
                        i0 = x[:, kt, 0:T].rearrange("p (c j) -> p c j", j=STEP)
                        i1 = n_r[:, 0:T].rearrange("p (c j) -> p c j", j=STEP)
                    else:
                        o, i0, i1 = hs[:, kt % 2, T:N], x[:, kt, T:N], n_r[:, T:N]
                    v.do(V.scalar_tensor_tensor(o, i0, gains[:, 2, kt:kt + 1], i1, ALU.mult, ALU.mult), f"hs{kt}")

        def s5pre_dve(v):
            V = nc.vector
            norm_s5_dve(v)
            v.e.wait_ge(s5_par, 16)
            are, aim, ldt = (par[:, k] for k in range(3))
            R = lambda k: sc[:, k]

            def op(ins, name=None):
                v.do(ins, name)

            v.after("ACT", "dt")
            op(V.tensor_tensor(R(1), are, R(0), ALU.mult))
            op(V.tensor_tensor(R(2), aim, R(0), ALU.mult), "rth")
            C1, C2, C3 = 6.28125, 0.0019350051879882812, 2 * math.pi - 6.28125 - 0.0019350051879882812
            for dst, shift in ((3, 0.0), (4, math.pi / 2)):
                op(V.tensor_scalar(R(5), R(2), 1.0 / (2 * math.pi), shift / (2 * math.pi), ALU.mult, ALU.add))
                op(V.tensor_scalar(R(5), R(5), 12582912.0, None, ALU.add))
                op(V.tensor_scalar(R(5), R(5), -12582912.0, None, ALU.add))
                op(V.scalar_tensor_tensor(R(6), R(5), -C1, R(2), ALU.mult, ALU.add))
                op(V.scalar_tensor_tensor(R(6), R(5), -C2, R(6), ALU.mult, ALU.add))
                op(V.scalar_tensor_tensor(R(6), R(5), -C3, R(6), ALU.mult, ALU.add))
                op(V.tensor_scalar(R(6), R(6), shift, math.pi * (1 - 1e-7), ALU.add, ALU.min))
                op(V.tensor_scalar(R(dst), R(6), -math.pi * (1 - 1e-7), None, ALU.max), "red")
            v.after("ACT", "trig")
            op(V.tensor_tensor(lam[:, 0, 1], R(7), R(9), ALU.mult))
            op(V.tensor_tensor(lam[:, 1, 1], R(7), R(8), ALU.mult))
            op(V.memset(lam[:, 0, 0], 1.0))
            op(V.memset(lam[:, 1, 0], 0.0))

            def cmul(ore, oim, ar, ai, br, bi, ta, tb):
                op(V.tensor_tensor(ta, ar, br, ALU.mult))
                op(V.tensor_tensor(tb, ai, bi, ALU.mult))
                op(V.tensor_tensor(tb, ta, tb, ALU.subtract))
                op(V.tensor_tensor(ta, ar, bi, ALU.mult))
                op(V.tensor_tensor(oim, ai, br, ALU.mult))
                op(V.tensor_tensor(oim, oim, ta, ALU.add))
                op(V.tensor_copy(ore, tb))
            for k in range(2, 9):
                cmul(lam[:, 0, k], lam[:, 1, k], lam[:, 0, k - 1], lam[:, 1, k - 1], lam[:, 0, 1], lam[:, 1, 1], R(10), R(11))
            op(V.tensor_tensor(R(10), are, are, ALU.mult))
            op(V.tensor_tensor(R(11), aim, aim, ALU.mult))
            op(V.tensor_tensor(R(10), R(10), R(11), ALU.add))
            op(V.reciprocal(R(10), R(10)))
            op(V.tensor_scalar(R(11), lam[:, 0, 1], -1.0, None, ALU.add))
            op(V.tensor_tensor(R(12), R(11), are, ALU.mult))
            op(V.tensor_tensor(R(13), lam[:, 1, 1], aim, ALU.mult))
            op(V.tensor_tensor(R(12), R(12), R(13), ALU.add))
            op(V.tensor_tensor(R(14), R(12), R(10), ALU.mult))
            op(V.tensor_tensor(R(12), lam[:, 1, 1], are, ALU.mult))
            op(V.tensor_tensor(R(13), R(11), aim, ALU.mult))
            op(V.tensor_tensor(R(12), R(12), R(13), ALU.subtract))
            op(V.tensor_tensor(R(15), R(12), R(10), ALU.mult))

            def unit(re, im):
                op(V.tensor_tensor(R(12), re, re, ALU.mult))
                op(V.tensor_tensor(R(13), im, im, ALU.mult))
                op(V.tensor_tensor(R(12), R(12), R(13), ALU.add))
                op(V.tensor_scalar(R(12), R(12), -0.5, 1.5, ALU.mult, ALU.add))
                op(V.tensor_tensor(re, re, R(12), ALU.mult))
                op(V.tensor_tensor(im, im, R(12), ALU.mult))
            op(V.tensor_copy(R(16), R(9)))
            op(V.tensor_copy(R(17), R(8)))
            unit(R(16), R(17))
            for _ in range(3):
                cmul(R(16), R(17), R(16), R(17), R(16), R(17), R(10), R(11))
                unit(R(16), R(17))
            v.do(V.tensor_scalar(R(18), R(1), float(STEP), None, ALU.mult), "r8")
            v.do(V.memset(kpad[:, :, :], 0.0))
            v.do(V.memset(uu[:, :, NBLK:UC], 0.0), "u0")

        def s5pre_act(a):
            norm_act(a)
            A = nc.scalar
            us = dr["us"].rearrange("(k p) n -> k p n", p=P)
            for kt in range(KT):
                a.after("DVE", f"hs{kt}")
                A.dma_start(us[kt], hs[:, kt % 2, :]).then_inc(u_store[kt % 2], 16)
            a.e.wait_ge(s5_par, 16)
            a.do(A.activation(sc[:, 0], par[:, 2], AF.Exp), "dt")
            a.after("DVE", "rth")
            a.do(A.activation(sc[:, 7], sc[:, 1], AF.Exp))
            a.after("DVE", "red")
            a.do(A.activation(sc[:, 8:10].rearrange("p a b -> p (a b)"), sc[:, 3:5].rearrange("p a b -> p (a b)"), AF.Sin), "trig")
            a.after("DVE", "r8")
            a.do(A.activation(sc[:, 19], sc[:, 18], AF.Exp), "m8")

        def s5pre_pe(p):
            norm_pe(p)

        def s5_dve(v):
            V = nc.vector
            rd = v.i
            pr = lambda k: sc[:, k, bass.ds(rd * PQ, PQ)]
            lm = lambda c, k: lam[:, c, k, bass.ds(rd * PQ, PQ)]

            def op(ins, name=None):
                v.do(ins, name)
            for k, src in enumerate((14, 15, 16, 17)):
                op(V.tensor_copy(pw[:, k // 2, k % 2], pr(src)))
            op(V.tensor_copy(pw[:, 2, 0], pr(19)))
            op(V.tensor_copy(pw[:, 3, 0], lm(0, 1)))
            op(V.tensor_copy(pw[:, 3, 1], lm(1, 1)))
            v.e.wait_ge(s5_par, v.i * 48 + 64)
            fr, fi = (pw[:, 0, k].unsqueeze(2).to_broadcast([P, PQ, G16]) for k in range(2))
            ta = t1[:, :, 0:G16]
            op(V.tensor_tensor(ta, bq[:, 0], fr, ALU.mult))
            op(V.tensor_tensor(bbq[:, 0], bq[:, 1], fi, ALU.mult))
            op(V.tensor_tensor(bbq[:, 0], ta, bbq[:, 0], ALU.subtract))
            op(V.tensor_tensor(ta, bq[:, 1], fr, ALU.mult))
            op(V.tensor_tensor(bbq[:, 1], bq[:, 0], fi, ALU.mult))
            op(V.tensor_tensor(bbq[:, 1], ta, bbq[:, 1], ALU.add))
            for k in range(9):
                lr = lm(0, k).unsqueeze(2).to_broadcast([P, PQ, G16])
                li = lm(1, k).unsqueeze(2).to_broadcast([P, PQ, G16])
                op(V.tensor_tensor(ta, cq[:, 0], lr, ALU.mult))
                op(V.tensor_tensor(cp[:, 0, :, k], cq[:, 1], li, ALU.mult))
                op(V.tensor_tensor(cp[:, 0, :, k], ta, cp[:, 0, :, k], ALU.subtract))
                op(V.tensor_tensor(ta, cq[:, 0], li, ALU.mult))
                op(V.tensor_tensor(cp[:, 1, :, k], cq[:, 1], lr, ALU.mult))
                op(V.scalar_tensor_tensor(cp[:, 1, :, k], cp[:, 1, :, k], -1.0, ta, ALU.mult, ALU.subtract), "cp")
            for k in range(STEP):
                lr = lm(0, k).unsqueeze(2).to_broadcast([P, PQ, G16])
                li = lm(1, k).unsqueeze(2).to_broadcast([P, PQ, G16])
                j = STEP - 1 - k
                op(V.tensor_tensor(ta, bbq[:, 0], lr, ALU.mult))
                op(V.tensor_tensor(bp[:, 0, :, j], bbq[:, 1], li, ALU.mult))
                op(V.tensor_tensor(bp[:, 0, :, j], ta, bp[:, 0, :, j], ALU.subtract))
                op(V.tensor_tensor(ta, bbq[:, 0], li, ALU.mult))
                op(V.tensor_tensor(bp[:, 1, :, j], bbq[:, 1], lr, ALU.mult))
                op(V.tensor_tensor(bp[:, 1, :, j], ta, bp[:, 1, :, j], ALU.add), "bp")
            op(V.memset(ee[:, 0, :, 0], 1.0))
            op(V.memset(ee[:, 1, :, 0], 0.0))
            ur, ui = pw[:, 1, 0], pw[:, 1, 1]
            n = 1
            while n < NBLK:
                er, ei = ee[:, 0, :, 0:n], ee[:, 1, :, 0:n]
                br = ur.unsqueeze(2).to_broadcast([P, PQ, n])
                bi = ui.unsqueeze(2).to_broadcast([P, PQ, n])
                a0, a1 = t2[:, 0, :, 0:n], t2[:, 1, :, 0:n]
                op(V.tensor_tensor(a0, er, br, ALU.mult))
                op(V.tensor_tensor(a1, ei, bi, ALU.mult))
                op(V.tensor_tensor(ee[:, 0, :, n:2 * n], a0, a1, ALU.subtract))
                op(V.tensor_tensor(a0, er, bi, ALU.mult))
                op(V.tensor_tensor(a1, ei, br, ALU.mult))
                op(V.tensor_tensor(ee[:, 1, :, n:2 * n], a0, a1, ALU.add))
                n *= 2
                if n < NBLK:
                    a0, a1 = t2[:, 0, :, 0], t2[:, 1, :, 0]
                    op(V.tensor_tensor(a0, ur, ur, ALU.mult))
                    op(V.tensor_tensor(a1, ui, ui, ALU.mult))
                    op(V.tensor_tensor(ui, ur, ui, ALU.mult))
                    op(V.tensor_scalar(ui, ui, 2.0, None, ALU.mult))
                    op(V.tensor_tensor(ur, a0, a1, ALU.subtract))
                    op(V.tensor_tensor(a0, ur, ur, ALU.mult))
                    op(V.tensor_tensor(a1, ui, ui, ALU.mult))
                    op(V.tensor_tensor(a0, a0, a1, ALU.add))
                    op(V.tensor_scalar(a0, a0, -0.5, 1.5, ALU.mult, ALU.add))
                    op(V.tensor_tensor(ur, ur, a0, ALU.mult))
                    op(V.tensor_tensor(ui, ui, a0, ALU.mult))
            v.after("ACT", "vv")
            vr, vi = vv[:, 0, :, 0:NBLK], vv[:, 1, :, 0:NBLK]
            er, ei = ee[:, 0], ee[:, 1]
            op(V.tensor_tensor(t2[:, 0], vr, er, ALU.mult))
            op(V.tensor_tensor(t2[:, 1], vi, ei, ALU.mult))
            op(V.tensor_tensor(t2[:, 0], t2[:, 0], t2[:, 1], ALU.add))
            op(V.tensor_tensor(t2[:, 1], vi, er, ALU.mult))
            op(V.tensor_tensor(vi, vr, ei, ALU.mult))
            op(V.tensor_tensor(t2[:, 1], t2[:, 1], vi, ALU.subtract))
            for c in range(2):
                for pi in range(PQ):
                    v.do(V.tensor_tensor_scan(vv[:, c, pi, 0:NBLK], pw[:, 2, 0, pi:pi + 1].to_broadcast([P, NBLK]), t2[:, c, pi], 0.0, ALU.mult, ALU.add))
            op(V.tensor_tensor(t2[:, 0], vr, er, ALU.mult))
            op(V.tensor_tensor(t2[:, 1], vi, ei, ALU.mult))
            op(V.tensor_tensor(t2[:, 0], t2[:, 0], t2[:, 1], ALU.subtract))
            op(V.tensor_tensor(t2[:, 1], vi, er, ALU.mult))
            op(V.tensor_tensor(vr, vr, ei, ALU.mult))
            op(V.tensor_tensor(t2[:, 1], t2[:, 1], vr, ALU.add))
            for c in range(2):
                v.do(V.tensor_copy(xp[:, c, :, 1:NBLK], t2[:, c, :, 0:NBLK - 1]))
                v.do(V.memset(xp[:, c, :, 0], 0.0))
                op(V.tensor_copy(sto[:, c, :, 0], t2[:, c, :, NBLK - 1]), "xp")
            lr = pw[:, 3, 0].unsqueeze(2).to_broadcast([P, PQ, B])
            li = pw[:, 3, 1].unsqueeze(2).to_broadcast([P, PQ, B])
            sr, si = xp[:, 0, :, NBLK:XC], xp[:, 1, :, NBLK:XC]
            b0, b1 = t2[:, 0, :, 0:B], t2[:, 1, :, 0:B]
            for c, (m0, m1, o_) in enumerate(((sr, si, ALU.subtract), (si, sr, ALU.add))):
                op(V.tensor_tensor(b0, m0, lr, ALU.mult))
                op(V.tensor_tensor(b1, m1, li, ALU.mult))
                op(V.tensor_tensor(b0, b0, b1, o_))
                op(V.tensor_tensor(sto[:, c, :, 1:1 + B], b0, vv[:, c, :, XC:UC], ALU.add), "sto")

        def s5_pe(p):
            p.after("DVE", "bp")
            for c in range(2):
                for pi in range(PQ):
                    ins = nc.tensor.transpose(ps[:, 4 + 2 * c, pi * P:(pi + 1) * P], bp[:, c, pi].rearrange("p a b -> p (a b)"), ident[:, :])
            p.do(ins, "wt")
            for g in range(2 * PQ):
                pi, g2 = g // 2, g % 2
                r = slice(64 * g2, 64 * g2 + 64)
                o = ps[0:G16, 2 * g2, pi * P:(pi + 1) * P]
                nc.tensor.matmul(o, bbq[r, 0, pi], cp[r, 0, pi, 0:STEP].rearrange("p a b -> p (a b)"), start=True, stop=False)
                ins = nc.tensor.matmul(o, bbq[r, 1, pi], cp[r, 1, pi, 0:STEP].rearrange("p a b -> p (a b)"), start=False, stop=True)
            p.do(ins, "K")
            p.after("ACT", "wt")
            p.e.wait_ge(u_load, p.i * 160 + 160)
            for c in range(2):
                for pi in range(PQ):
                    for g2 in range(2):
                        r = slice(64 * g2, 64 * g2 + 64)
                        ins = nc.tensor.matmul(ps[r, 3 * c + pi // 3, (pi % 3) * UC:(pi % 3 + 1) * UC], wt[:, c, pi, r], uu[:, 2 * pi + g2, :], start=True, stop=True)
            p.do(ins, "vv")
            p.after("DVE", "xp")
            p.after("ACT", "vv")
            p.e.wait_ge(h_shift, p.i * 128 + 128)
            for g2 in range(2):
                for pi in range(PQ):
                    g = 2 * pi + g2
                    r = slice(64 * g2, 64 * g2 + 64)
                    o = ps[:, NVB * g2 + pi // 3, (pi % 3) * XC:(pi % 3 + 1) * XC]
                    for c in range(2):
                        nc.tensor.matmul(o, cp[r, c, pi, 1:9].rearrange("p a b -> p (a b)"), xp[r, c, pi, :], start=c == 0, stop=False)
                    ins = nc.tensor.matmul(o, ht[:, g, :], uu[:, g, 0:XC], start=False, stop=True)
                p.do(ins, f"y{g2}")

        def s5_act(a):
            A = nc.scalar
            a.after("PE", "K")
            for g2 in range(2):
                dst = kpad[:, :, (STEP - 1) * G16:].rearrange("p (q g) n -> p q g n", g=2)[:, :, g2]
                a.do(A.activation(dst, ps[0:G16, 2 * g2, :].rearrange("p (q n) -> p q n", n=P), AF.Copy), "kpad")
            for j in range(STEP):
                A.dma_start(ht[G16 * j:G16 * (j + 1), :, :], kpad[:, :, (STEP - 1 - j) * G16:(2 * STEP - 1 - j) * G16]).then_inc(h_shift, 16)
            a.after("PE", "wt")
            for c in range(2):
                a.do(A.activation(wt[:, c].rearrange("p a b -> p (a b)"), ps[:, 4 + 2 * c, :], AF.Copy), "wt")
            a.after("PE", "vv")
            for c in range(2):
                for b0 in range(NVB):
                    np_ = min(3, PQ - 3 * b0)
                    a.do(A.activation(vv[:, c, 3 * b0:3 * b0 + np_], ps[:, 3 * c + b0, 0:np_ * UC].rearrange("p (a b) -> p a b", b=UC), AF.Copy), "vv")
            a.after("PE", "y1")
            for g2 in range(2):
                for b0 in range(NVB):
                    p0, p1 = 3 * b0, min(3 * b0 + 3, PQ)
                    y3 = ps[:, NVB * g2 + b0, 0:(p1 - p0) * XC].rearrange("p (a b) -> p a b", b=XC)
                    du = uu[:, :, 0:NBLK].rearrange("p (q g) n -> p q g n", g=2)[:, p0:p1, g2]
                    ds_ = ysmp[:, :, :].rearrange("p (q g) n -> p q g n", g=2)[:, p0:p1, g2]
                    a.do(A.activation(du, y3[:, :, 0:NBLK], AF.Copy), "ysb")
                    a.do(A.activation(ds_, y3[0:G16, :, NBLK:XC], AF.Copy), "ysb")
            ys = dr["ys"].rearrange("(r g c) n -> r c g n", r=SR, c=G16)
            for i_ in range(STEP):
                A.dma_start(ys[a.i, :, :, i_ * NBLK:(i_ + 1) * NBLK], uu[G16 * i_:G16 * (i_ + 1), :, 0:NBLK]).then_inc(y_store, 16)
            A.dma_start(ys[a.i, :, :, T:N], ysmp[:, :, :]).then_inc(y_store, 16)
            a.after("DVE", "sto")
            A.dma_start(dr["s5o"][a.i], sto[:, :, :, :]).then_inc(s5_out, 16)
            a.e.wait_ge(y_store, a.i * 144 + 144)
            a.e.wait_ge(s5_out, a.i * 16 + 16)
            a.mark()

        def gel_dve(v):
            V = nc.vector
            v.e.wait_ge(s5_par, 32 + 48 * SR)
            for kt in range(KT):
                s = kt % 2
                v.e.wait_ge(y_load[s], 32 * (kt // 2) + 32)
                v.do(V.scalar_tensor_tensor(yf[:, s, :], hd[:, s, :], dsk[:, kt:kt + 1], yf[:, s, :], ALU.mult, ALU.add), f"yd{kt}")
                v.after("ACT", f"hi{kt}")
                v.do(V.tensor_tensor(hlo[:, kt, :], yg[:, s, :], hhi[:, kt, :].bitcast(F32), ALU.subtract), f"lo{kt}")

        def glu_pe(p):
            project(p, 0, 0, "a.")
            project(p, 1, 1, "b.")

        def glu_act(a):
            for n in range(NC3):
                if n < 2:
                    a.after("PE", f"b.{n}")
                else:
                    a.unit_done(1)
                a.do(nc.scalar.activation(rf["sg"][:, 0, blk(n)], ps[:, 3 + n, 0:NB], AF.Sigmoid), f"sig{n}")

        def glu_dve(v):
            V = nc.vector
            for n in range(NC3):
                if n < 2:
                    v.after("PE", f"a.{n}")
                else:
                    v.unit_done(0)
                v.after("ACT", f"sig{n}")
                v.do(V.tensor_tensor(rf["ab"][:, 0, blk(n)], ps[:, n, 0:NB], rf["sg"][:, 0, blk(n)], ALU.mult))
                xm = x[:, bass.ds(v.i, 1), blk(n)].rearrange("p a n -> p (a n)")
                v.do(V.tensor_tensor(xm, xm, rf["ab"][:, 0, blk(n)], ALU.add))

        def fin_dve(v):
            V = nc.vector
            v.after("ACT", "rms")
            v.do(V.reciprocal(nr[:, :], nr[:, :]))
            for kt in range(KT):
                v.do(V.scalar_tensor_tensor(x[:, kt, :], x[:, kt, :], gains[:, 4, kt:kt + 1], nr[:, :], ALU.mult, ALU.mult), f"y{kt}")

        PH = [("prolog", 1), ("mix", HQK), ("n1", 1), ("ffn0", FT // 2), ("s5pre", 1), ("s5", SR), ("gel", 1), ("glu", KT), ("n3", 1), ("ffn1", FT // 2), ("fin", 1)]
        nothing = lambda e: None
        base_nrm = (nsq, nr, nh)

        block = ctx.enter_context(nc.Block())

        def program(who, eng, table):
            nonlocal nsq, nr, nh
            E = Eng(who, eng)
            for ph, cnt in PH:
                if ph == "prolog":
                    nsq, nr, nh = base_nrm
                else:
                    nsq, nr, nh = n_sq, n_r, n_h
                E.run(ph, cnt, table[ph])
            return E

        @block.sync
        def _(sp):
            for k, (dst, src) in enumerate(((gains, "gains"), (alog, "alog"), (cw, "cw"), (ng, "ng"))):
                sp.dma_start(dst[tuple([slice(None)] * len(dst.shape))], dr[src]).then_inc(in_par, 16)
            sp.dma_start(x[:, :, :], dr["x"]).then_inc(in_x, 16)
            for n in range(2):
                sp.dma_start(wraw[:, n, :], dr["w"][n]).then_inc(w_loaded[n], 16)
            with sp.Fori(1, N_UNITS // 2) as i:
                for n in range(2):
                    sp.wait_ge(w_split, 2 * i + (n - 1))
                    sp.dma_start(wraw[:, n, :], dr["w"][2 * i + n]).then_inc(w_loaded[n], 16)
            sp.wait_ge(w_split, N_UNITS - 2)
            sp.dma_start(wraw[:, 0, :], dr["w"][N_UNITS - 1]).then_inc(w_loaded[0], 16)

        @block.gpsimd
        def _(pool):
            G = nc.gpsimd
            G.memset(ones[:, :], 1.0)
            G.memset(wtick[:, :], 0.0)
            G.memset(eps_t[:, 0:1], EPS).then_inc(const_ready, 1)
            G.memset(lev[:, :, :], -1.0).then_inc(const_ready, 1)
            pool.wait_ge(const_ready, 2)

            def select(out, in_, pattern, base, cm, op=ALU.is_ge, fill=0.0):
                return G.affine_select(out=out, in_=in_, compare_op=op, fill=fill, base=base, pattern=pattern, channel_multiplier=cm)
            select(ident[:, :], ones[:, :], [[-1, P]], 0, 1, ALU.is_equal)
            select(upin[:, :], ones[:, :], [[1, P]], 0, -1)
            select(slow[:, :], ones[:, :], [[-1, P]], -1, 1).then_inc(const_ready, 1)
            for l in range(7):
                s = 1 << l
                nb_ = P // (2 * s)
                m = lev[:, 1 + l].rearrange("p (a t b) -> p a t b", t=2, b=s)
                G.memset(m[:, :, 0, :], 0.0).then_inc(const_ready, 1) if l == 0 else G.memset(m[:, :, 0, :], 0.0).then_inc(lev_done, 1)
            pool.wait_ge(const_ready, 4)
            pool.wait_ge(lev_done, 6)
            for l in range(7):
                s = 1 << l
                m = lev[:, 1 + l].rearrange("p (a t b) -> p a t b", t=2, b=s)[:, :, 1, :]
                select(m, m, [[-2 * s, P // (2 * s)], [0, s]], 0, 1).then_inc(lev_done, 1)
                pool.wait_ge(lev_done, 6 + 2 * l + 1)
                select(m, m, [[2 * s, P // (2 * s)], [0, s]], s - 1, -1).then_inc(lev_done, 1)
            m = lev[:, 0].rearrange("p (a t) -> p a t", t=2)
            select(m, m, [[-2, P // 2], [-1, 2]], -1, 1, ALU.is_equal).then_inc(lev_done, 1)
            pool.wait_ge(lev_done, 21)
            G.memset(m[:, :, 1], 0.0).then_inc(const_ready, 1)
            pool.wait_ge(const_ready, 5)
            G.memset(eps_t[:, 2:3], 0.0).then_inc(const_ready, 1)

            def split(n, slot, first):
                i2 = n
                pool.wait_ge(w_loaded[slot], i2[0])
                if not first:
                    pool.wait_ge(w_used, i2[1])
                G.tensor_tensor(wtick[:, 1:2], wtick[:, 0:1], wtick[:, 0:1], ALU.add)
                G.tensor_copy(whi[:, slot, :], wraw[:, slot, :]).then_inc(w_hi, 1)
                pool.wait_ge(w_hi, i2[2])
                G.tensor_tensor(wlo[:, slot, :], wraw[:, slot, :], whi[:, slot, :].bitcast(F32), ALU.subtract).then_inc(w_split, 1)
            for n in range(2):
                split((16, 0, n + 1), n, True)
            with pool.Fori(1, N_UNITS // 2) as i:
                for n in range(2):
                    split((i * 16 + 16, 2 * i + (n - 1), 2 * i + (n + 1)), n, False)
            split((16 * (N_UNITS // 2 + 1), N_UNITS - 2, N_UNITS), 0, False)

        act_t = {"prolog": pro_act, "mix": mix_act, "n1": lambda a: (norm_act(a), norm_hi(a)), "ffn0": ffn_act(rf), "s5pre": s5pre_act, "s5": s5_act,
                 "gel": nothing, "glu": glu_act, "n3": lambda a: (norm_act(a), norm_hi(a)), "ffn1": ffn_act(rf), "fin": norm_act}
        dve_t = {"prolog": pro_dve, "mix": mix_dve, "n1": lambda v: norm_dve(v, 1), "ffn0": ffn_dve(rf), "s5pre": s5pre_dve, "s5": s5_dve,
                 "gel": gel_dve, "glu": glu_dve, "n3": lambda v: norm_dve(v, 3), "ffn1": ffn_dve(rf), "fin": fin_dve}
        pe_t = {"prolog": pro_pe, "mix": mix_pe, "n1": norm_pe, "ffn0": ffn_pe(rf), "s5pre": s5pre_pe, "s5": s5_pe,
                "gel": nothing, "glu": glu_pe, "n3": norm_pe, "ffn1": ffn_pe(rf), "fin": norm_pe}

        def with_dma(ph, fn):
            def body(a):
                A = nc.scalar
                if ph == "mix":
                    A.dma_start(cst[:, :, :, :], dr["cin"][a.i]).then_inc(in_conv, 16)
                    fn(a)
                elif ph == "s5pre":
                    A.dma_start(par[:, :, :], dr["par"]).then_inc(s5_par, 16)
                    fn(a)
                    for n in range(2):
                        a.e.wait_ge(u_store[n], 16 * KT // 2)
                    a.mark()
                elif ph == "s5":
                    A.dma_start(bq[:, :, :, :], dr["b"][a.i]).then_inc(s5_par, 16)
                    A.dma_start(cq[:, :, :, :], dr["c"][a.i]).then_inc(s5_par, 16)
                    A.dma_start(xp[:, :, :, NBLK:XC], dr["s5i"][a.i]).then_inc(s5_par, 16)
                    us = dr["us"].rearrange("(r g c) n -> r c g n", r=SR, c=G16)
                    for j in range(STEP):
                        A.dma_start(uu[G16 * j:G16 * (j + 1), :, 0:NBLK], us[a.i, :, :, j * NBLK:(j + 1) * NBLK]).then_inc(u_load, 16)
                    A.dma_start(uu[0:G16, :, NBLK:XC], us[a.i, :, :, T:N]).then_inc(u_load, 16)
                    A.dma_start(uu[P - G16:P, :, XC:UC], us[a.i, :, :, T:N]).then_inc(u_load, 16)
                    fn(a)
                elif ph == "gel":
                    A.dma_start(dsk[:, :], dr["d"]).then_inc(s5_par, 16)
                    ys = dr["ys"].rearrange("(k p) n -> k p n", p=P)
                    us = dr["us"].rearrange("(k p) n -> k p n", p=P)
                    for kt in range(2):
                        A.dma_start(yf[:, kt, :], ys[kt]).then_inc(y_load[kt], 16)
                        A.dma_start(hd[:, kt, :], us[kt]).then_inc(y_load[kt], 16)
                    for kt in range(KT):
                        gel_act1(a, kt)
                        if kt + 2 < KT:
                            a.after("ACT", f"ge{kt}")
                            A.dma_start(yf[:, kt % 2, :], ys[kt + 2]).then_inc(y_load[kt % 2], 16)
                            A.dma_start(hd[:, kt % 2, :], us[kt + 2]).then_inc(y_load[kt % 2], 16)
                elif ph == "fin":
                    fn(a)
                    for kt in range(KT):
                        a.after("DVE", f"y{kt}")
                        A.dma_start(dr["y"][:, kt], x[:, kt, :]).then_inc(out_y, 16)
                    a.e.wait_ge(out_y, 16 * KT)
                else:
                    fn(a)
            return body

        def gel_act1(a, kt):
            A = nc.scalar
            s = kt % 2
            if kt >= 2:
                a.after("DVE", f"lo{kt - 2}")
            a.after("DVE", f"yd{kt}")
            a.do(A.activation(yg[:, s, 0:T].rearrange("p (c j) -> p c j", j=STEP), yf[:, s, 0:T].rearrange("p (j c) -> p c j", j=STEP), AF.Gelu_apprx_tanh))
            a.do(A.activation(yg[:, s, T:N], yf[:, s, T:N], AF.Gelu_apprx_tanh), f"ge{kt}")
            a.do(A.activation(hhi[:, kt, :], yg[:, s, :], AF.Copy), f"hi{kt}")

        @block.scalar
        def _(act):
            program("ACT", act, {ph: with_dma(ph, act_t[ph]) for ph, _ in PH})

        @block.vector
        def _(dve):
            program("DVE", dve, dve_t)

        @block.tensor
        def _(pe):
            program("PE", pe, pe_t)


def _shapes():
    return {
        "x": (P, KT, N), "w": (N_UNITS, P, UW), "gains": (P, 5, KT), "alog": (P, 2, HV), "cw": (P, HQK, 4, CONVW),
        "ng": (P, 1), "cin": (HQK, P, 4, 3, B), "sin": (HQK, P, 2 * B, P), "par": (P, 3, NPAIR),
        "b": (SR, P, 2, PQ, G16), "c": (SR, P, 2, PQ, G16), "s5i": (SR, P, 2, PQ, B), "d": (P, KT),
    }, {
        "y": (P, KT, N), "sp": (HQK, P, 2, P), "sout": (HQK, P, 2 * B, P), "cpo": (HQK, P, 4, 3),
        "cso": (HQK, P, 4, 3, B), "s5o": (SR, P, 2, PQ, 1 + B),
    }


def program(nc, plan):
    ins, outs = _shapes()
    dr = {k: nc.dram_tensor("in_" + k, s, F32, kind="ExternalInput").ap() for k, s in ins.items()}
    dr |= {k: nc.dram_tensor("out_" + k, s, F32, kind="ExternalOutput").ap() for k, s in outs.items()}
    dr |= {k: nc.dram_tensor("scr_" + k, (D, N), F32, kind="Internal").ap() for k in ("us", "ys")}
    build(nc, dr, plan)


def kernel(**inp):
    import concourse.bacc as _bacc
    from concourse.bass_utils import run_bass_kernel_spmd as _run

    I = {k: np.asarray(v) for k, v in inp.items()}
    A = {}
    xs = np.concatenate([I["x_prompt"][0], I["x_sample"][:, 0]], 0)
    A["x"] = xs.T.reshape(KT, P, N).transpose(1, 0, 2)

    def proj_unit(w, c):
        return w[:, c:c + P].reshape(KT, P, P).transpose(1, 0, 2).reshape(P, UW)

    def out_unit(w, k, half):
        return w[k * P:(k + 2) * P, half * 512:(half + 1) * 512].reshape(2, P, 512).transpose(1, 0, 2).reshape(P, UW)

    wi, wo = I["w_dn_in"][0], I["w_dn_out"][0]
    kd, vd = HQK * P, HV * P
    ba = np.zeros((D, P), np.float32)
    ba[:, 0:2 * HV] = wi[:, 2 * kd + 2 * vd:]
    units = [proj_unit(ba, 0)]
    for g in range(HQK):
        for c in (kd + g * P, g * P, 2 * kd + 2 * g * P, 2 * kd + (2 * g + 1) * P, 2 * kd + vd + 2 * g * P, 2 * kd + vd + (2 * g + 1) * P):
            units.append(proj_unit(wi, c))
        units += [out_unit(wo, 2 * g, 0), out_unit(wo, 2 * g, 1)]

    def ffn(l):
        w1, w2 = I["w_ffn_in"][l], I["w_ffn_out"][l]
        for f in range(0, FT, 2):
            for j in range(2):
                units.append(proj_unit(w1, (f + j) * P))
                units.append(proj_unit(w1, FF + (f + j) * P))
            units.extend([out_unit(w2, f, 0), out_unit(w2, f, 1)])
    ffn(0)
    for m in range(KT):
        units.append(proj_unit(I["w_s5_glu"][0], m * P))
        units.append(proj_unit(I["w_s5_glu"][0], D + m * P))
    ffn(1)
    A["w"] = np.stack(units)
    nm, nf = I["norm_mix_g"], I["norm_ffn_g"]
    A["gains"] = np.stack([nm[0], nf[0], nm[1], nf[1], I["final_norm_g"]]).reshape(5, KT, P).transpose(2, 0, 1)
    A["alog"] = np.broadcast_to(np.stack([I["dn_a_log"][0], I["dn_dt_bias"][0]]), (P, 2, HV))

    def tiles(a):
        t = a.reshape(a.shape[:-1] + (32, P))
        order = [[HQK + g, g, 2 * HQK + 2 * g, 2 * HQK + 2 * g + 1] for g in range(HQK)]
        return t[..., np.array(order), :]
    A["cw"] = tiles(I["dn_conv_w"][0]).transpose(3, 1, 2, 0)
    A["ng"] = I["dn_norm_g"][0].reshape(P, 1)
    A["cin"] = tiles(I["state_dn_conv"][0]).transpose(2, 4, 3, 1, 0)
    A["sin"] = I["state_dn_ssm"][0].reshape(B, HQK, 2, P, P).transpose(1, 3, 2, 0, 4).reshape(HQK, P, 2 * B, P)

    def gp(a):
        return np.moveaxis(a.reshape((NPAIR, 2, 64) + a.shape[2:]), 0, 2).reshape((P, NPAIR) + a.shape[2:])

    def rounds(re, im):
        t = np.stack([gp(re), gp(im)], 1)
        return t.reshape(P, 2, SR, PQ, t.shape[-1]).transpose(2, 0, 1, 3, 4)
    ldt = np.broadcast_to(I["s5_log_dt"][0][:, None], (64, 64))
    A["par"] = np.stack([gp(I["s5_a_re"][0]), gp(I["s5_a_im"][0]), gp(ldt)], 1)
    A["b"] = rounds(I["s5_b_re"][0], I["s5_b_im"][0])
    A["c"] = rounds(I["s5_c_re"][0].transpose(0, 2, 1), I["s5_c_im"][0].transpose(0, 2, 1))
    A["s5i"] = rounds(I["state_s5_re"][0].transpose(1, 2, 0), I["state_s5_im"][0].transpose(1, 2, 0))
    A["d"] = I["s5_d"][0].reshape(KT, P).T
    plan = {}
    for _ in range(2):
        plan["missing"] = set()
        nc = _bacc.Bacc("TRN2", target_bir_lowering=False, num_devices=1)
        program(nc, plan)
    assert not plan["missing"], plan["missing"]
    arrays = {"in_" + k: np.ascontiguousarray(v) for k, v in A.items()}
    r = _run(nc, [arrays], core_ids=[0]).results[0]
    o = {k: np.asarray(r["out_" + k]).reshape(s) for k, s in _shapes()[1].items()}
    y = o["y"].transpose(2, 1, 0).reshape(N, D)

    def untile(a):
        a = np.moveaxis(a, 1, -1)
        q = a[:, 1].reshape((HQK,) + a.shape[2:])
        k = a[:, 0]
        v = a[:, 2:4].reshape((HV,) + a.shape[2:])
        t = np.concatenate([q, k, v], 0)
        t = np.moveaxis(t, 0, -2)
        return np.ascontiguousarray(t.reshape(t.shape[:-2] + (32 * P,)))
    conv_p = untile(o["cpo"])[None, None]
    conv_s = untile(o["cso"]).transpose(1, 0, 2)[None]
    ssm_p = o["sp"].transpose(0, 2, 1, 3).reshape(1, 1, HV, P, P)
    ssm_s = o["sout"].reshape(HQK, P, 2, B, P).transpose(3, 0, 2, 1, 4).reshape(1, B, HV, P, P)
    st = o["s5o"].reshape(SR, 2, 64, 2, PQ, 1 + B).transpose(3, 5, 0, 4, 1, 2).reshape(2, 1 + B, 64, 64)
    c = np.ascontiguousarray
    return (c(y[:T])[None], c(y[T:])[:, None], c(ssm_p), c(conv_p), c(st[0, 0:1])[None], c(st[1, 0:1])[None],
            c(ssm_s), c(conv_s), c(st[0, 1:])[None], c(st[1, 1:])[None])
```
